# Optimizing a Trainium2 kernel written in Bass

```python
import math
import jax, jax.numpy as jnp
from jax import lax
import numpy as np

D_MODEL = 1024
BATCH = 1
SEQ = 2048
DEPTH = 1

D_MIX = D_MODEL
GLA_WIDTH = D_MIX // 2
GLA_HEADS = 4
GLA_DV = GLA_WIDTH // GLA_HEADS
GLA_DK = GLA_DV // 2
GLA_KW = GLA_HEADS * GLA_DK
GLA_GATE_RANK = 16
GLA_GATE_NORM = 16.0
SSD_WIDTH = D_MIX - GLA_WIDTH
SSD_HEADDIM = 64
SSD_HEADS = SSD_WIDTH // SSD_HEADDIM
SSD_GROUPS = 2
SSD_HPG = SSD_HEADS // SSD_GROUPS
SSD_STATE = 128
SSD_CONV = 4
SSD_CONV_CH = SSD_WIDTH + 2 * SSD_GROUPS * SSD_STATE
CHUNK = 64
IN_SPLITS = [GLA_KW, GLA_KW, GLA_WIDTH, GLA_WIDTH, GLA_GATE_RANK,
             SSD_WIDTH, SSD_CONV_CH, SSD_HEADS]
D_IN = sum(IN_SPLITS)
N_EXPERTS = 32
TOP_K = 4
D_FF = D_MODEL
SWIGLU_LIMIT = 7.0
SWIGLU_ALPHA = 1.702
EPS = 1e-6
GROUP_EPS = 1e-5

kernel_name = "hymba_gla_ssd_moe_block"

def rmsnorm(x, w, eps=EPS):
    xf = x.astype(jnp.float32)
    y = xf * lax.rsqrt(jnp.mean(xf * xf, axis=-1, keepdims=True) + eps)
    return (y * w.astype(jnp.float32)).astype(x.dtype)

def gla_chunked(q, k, v, log_a):
    bsz, seqlen, heads, _ = q.shape
    dv = v.shape[-1]
    n = seqlen // CHUNK

    def to_chunks(t):
        return jnp.moveaxis(t.reshape(bsz, n, CHUNK, heads, t.shape[-1]), 1, 0).transpose(0, 1, 3, 2, 4)

    bcum = jnp.cumsum(to_chunks(log_a), axis=3)
    mask = jnp.tril(jnp.ones((CHUNK, CHUNK), bool))[:, :, None]

    def step(state, inp):
        qc, kc, vc, bc = inp
        inter = jnp.einsum('bhcd,bhdv->bhcv', qc * jnp.exp(bc), state)
        diff = bc[:, :, :, None, :] - bc[:, :, None, :, :]
        decay = jnp.where(mask, jnp.exp(jnp.where(mask, diff, 0.0)), 0.0)
        scores = jnp.einsum('bhid,bhjd,bhijd->bhij', qc, kc, decay)
        intra = jnp.einsum('bhij,bhjv->bhiv', scores, vc)
        b_last = bc[:, :, -1, :]
        state = state * jnp.exp(b_last)[..., None] + jnp.einsum(
            'bhcd,bhcv->bhdv', kc * jnp.exp(b_last[:, :, None, :] - bc), vc)
        return state, inter + intra

    s0 = jnp.zeros((bsz, heads, q.shape[-1], dv), jnp.float32)
    _, o = lax.scan(step, s0, (to_chunks(q), to_chunks(k), to_chunks(v), bcum))
    return o.transpose(1, 0, 3, 2, 4).reshape(bsz, seqlen, heads, dv)

def ssd_chunked(x, dt, a_neg, bm, cm):
    bsz, seqlen = x.shape[:2]
    n = seqlen // CHUNK

    def to_chunks(t):
        return jnp.moveaxis(t.reshape(bsz, n, CHUNK, *t.shape[2:]), 1, 0)

    acum = jnp.cumsum(to_chunks(dt * a_neg), axis=2)
    mask = jnp.tril(jnp.ones((CHUNK, CHUNK), bool))[None, :, :, None, None]

    def step(state, inp):
        xc, dtc, ac, bc, cc = inp
        seg = ac[:, :, None] - ac[:, None, :]
        lmat = jnp.where(mask, jnp.exp(jnp.where(mask, seg, 0.0)), 0.0)
        cb = jnp.einsum('bign,bjgn->bijg', cc, bc)
        intra = jnp.einsum('bijg,bijgh,bjghp->bighp', cb, lmat, xc * dtc[..., None])
        inter = jnp.einsum('bign,bghpn->bighp', cc, state) * jnp.exp(ac)[..., None]
        a_last = ac[:, -1]
        wgt = jnp.exp(a_last[:, None] - ac) * dtc
        state = state * jnp.exp(a_last)[..., None, None] + jnp.einsum(
            'bjgn,bjgh,bjghp->bghpn', bc, wgt, xc)
        return state, intra + inter

    s0 = jnp.zeros((bsz, SSD_GROUPS, SSD_HPG, SSD_HEADDIM, SSD_STATE), jnp.float32)
    _, y = lax.scan(step, s0, (to_chunks(x), to_chunks(dt), acum, to_chunks(bm), to_chunks(cm)))
    return jnp.moveaxis(y, 0, 1).reshape(x.shape)

def moe_ffn(h, router_w, router_b, w_gate, b_gate, w_up, b_up, w_down, b_down):
    bsz, seqlen, d = h.shape
    hf = h.reshape(-1, d)
    t = hf.shape[0]
    logits = hf.astype(jnp.float32) @ router_w.astype(jnp.float32) + router_b.astype(jnp.float32)
    top_vals, top_idx = lax.top_k(logits, TOP_K)
    gates = jax.nn.softmax(top_vals, axis=-1)
    flat_e = top_idx.reshape(-1)
    order = jnp.argsort(flat_e)
    tok = order // TOP_K
    sorted_e = flat_e[order]
    group_sizes = jnp.bincount(flat_e, length=N_EXPERTS).astype(jnp.int32)
    xs = hf[tok]
    gate = lax.ragged_dot(xs, w_gate, group_sizes) + b_gate[sorted_e]
    up = lax.ragged_dot(xs, w_up, group_sizes) + b_up[sorted_e]
    gate = jnp.minimum(gate, SWIGLU_LIMIT)
    up = jnp.clip(up, -SWIGLU_LIMIT, SWIGLU_LIMIT)
    act = (up + 1.0) * (gate * jax.nn.sigmoid(SWIGLU_ALPHA * gate))
    out = lax.ragged_dot(act, w_down, group_sizes) + b_down[sorted_e]
    wsel = gates.reshape(-1)[order].astype(out.dtype)
    y = jnp.zeros((t, d), out.dtype).at[tok].add(out * wsel[:, None])
    return y.reshape(bsz, seqlen, d).astype(h.dtype)

def setup_inputs(seed: int = 0) -> dict:
    key = jax.random.key(seed)
    ks = jax.random.split(key, 24)
    f32 = jnp.float32

    def nrm(k, shape, fan_in):
        return jax.random.normal(k, shape, f32) * (fan_in ** -0.5)

    def gain(k, shape):
        return 1.0 + 0.02 * jax.random.normal(k, shape, f32)

    dt = jnp.exp(jax.random.uniform(ks[9], (DEPTH, SSD_HEADS), f32, math.log(1e-3), math.log(1e-1)))
    return {
        "x": jax.random.normal(ks[0], (BATCH, SEQ, D_MODEL), f32),
        "norm_mix_w": gain(ks[1], (DEPTH, D_MODEL)),
        "w_in": nrm(ks[2], (DEPTH, D_MODEL, D_IN), D_MODEL),
        "gla_w_alpha_up": nrm(ks[3], (DEPTH, GLA_GATE_RANK, GLA_KW), GLA_GATE_RANK),
        "gla_b_alpha": 0.1 * jax.random.normal(ks[4], (DEPTH, GLA_KW), f32) + 2.0,
        "gla_norm_w": gain(ks[5], (DEPTH, GLA_WIDTH)),
        "ssd_conv_w": nrm(ks[6], (DEPTH, SSD_CONV, SSD_CONV_CH), SSD_CONV),
        "ssd_conv_b": 0.02 * jax.random.normal(ks[7], (DEPTH, SSD_CONV_CH), f32),
        "ssd_dt_bias": dt + jnp.log(-jnp.expm1(-dt)),
        "ssd_A_log": jnp.log(jax.random.uniform(ks[10], (DEPTH, SSD_HEADS), f32, 1.0, 16.0)),
        "ssd_D": gain(ks[11], (DEPTH, SSD_HEADS)),
        "ssd_norm_w": gain(ks[12], (DEPTH, SSD_WIDTH)),
        "w_out": nrm(ks[13], (DEPTH, D_MIX, D_MODEL), D_MIX),
        "norm_ffn_w": gain(ks[14], (DEPTH, D_MODEL)),
        "router_w": nrm(ks[15], (DEPTH, D_MODEL, N_EXPERTS), D_MODEL),
        "router_b": 0.01 * jax.random.normal(ks[16], (DEPTH, N_EXPERTS), f32),
        "moe_w_gate": nrm(ks[17], (DEPTH, N_EXPERTS, D_MODEL, D_FF), D_MODEL),
        "moe_b_gate": 0.02 * jax.random.normal(ks[18], (DEPTH, N_EXPERTS, D_FF), f32),
        "moe_w_up": nrm(ks[19], (DEPTH, N_EXPERTS, D_MODEL, D_FF), D_MODEL),
        "moe_b_up": 0.02 * jax.random.normal(ks[20], (DEPTH, N_EXPERTS, D_FF), f32),
        "moe_w_down": nrm(ks[21], (DEPTH, N_EXPERTS, D_FF, D_MODEL), D_FF),
        "moe_b_down": 0.02 * jax.random.normal(ks[22], (DEPTH, N_EXPERTS, D_MODEL), f32),
        "final_norm_w": gain(ks[23], (D_MODEL,)),
    }

def reference(x, norm_mix_w, w_in, gla_w_alpha_up, gla_b_alpha, gla_norm_w, ssd_conv_w, ssd_conv_b,
              ssd_dt_bias, ssd_A_log, ssd_D, ssd_norm_w, w_out, norm_ffn_w, router_w, router_b,
              moe_w_gate, moe_b_gate, moe_w_up, moe_b_up, moe_w_down, moe_b_down, final_norm_w):
    bsz, seqlen, _ = x.shape
    f32 = jnp.float32
    split_pts = list(np.cumsum(IN_SPLITS)[:-1])
    for l in range(DEPTH):
        h = rmsnorm(x, norm_mix_w[l])
        proj = h @ w_in[l]
        q, k, v, g, a_low, z, xbc, dt_raw = jnp.split(proj, split_pts, axis=-1)

        qh = q.astype(f32).reshape(bsz, seqlen, GLA_HEADS, GLA_DK) * (GLA_DK ** -0.5)
        kh = k.astype(f32).reshape(bsz, seqlen, GLA_HEADS, GLA_DK)
        vh = v.astype(f32).reshape(bsz, seqlen, GLA_HEADS, GLA_DV)
        log_a = jax.nn.log_sigmoid((a_low @ gla_w_alpha_up[l] + gla_b_alpha[l]).astype(f32)) / GLA_GATE_NORM
        o = gla_chunked(qh, kh, vh, log_a.reshape(bsz, seqlen, GLA_HEADS, GLA_DK))
        o = o * lax.rsqrt(jnp.mean(o * o, axis=-1, keepdims=True) + GROUP_EPS)
        gla_out = o.reshape(bsz, seqlen, GLA_WIDTH) * gla_norm_w[l].astype(f32) * jax.nn.silu(g.astype(f32))

        conv = lax.conv_general_dilated(
            xbc, ssd_conv_w[l][:, None, :], window_strides=(1,), padding=[(SSD_CONV - 1, 0)],
            dimension_numbers=('NWC', 'WIO', 'NWC'), feature_group_count=SSD_CONV_CH)
        xbc_act = jax.nn.silu((conv + ssd_conv_b[l]).astype(f32))
        xs, bm, cm = jnp.split(xbc_act, [SSD_WIDTH, SSD_WIDTH + SSD_GROUPS * SSD_STATE], axis=-1)
        xs = xs.reshape(bsz, seqlen, SSD_GROUPS, SSD_HPG, SSD_HEADDIM)
        bm = bm.reshape(bsz, seqlen, SSD_GROUPS, SSD_STATE)
        cm = cm.reshape(bsz, seqlen, SSD_GROUPS, SSD_STATE)
        dt = jax.nn.softplus(dt_raw.astype(f32) + ssd_dt_bias[l].astype(f32))
        dt = dt.reshape(bsz, seqlen, SSD_GROUPS, SSD_HPG)
        a_neg = -jnp.exp(ssd_A_log[l].astype(f32)).reshape(SSD_GROUPS, SSD_HPG)
        y = ssd_chunked(xs, dt, a_neg, bm, cm)
        y = y + ssd_D[l].astype(f32).reshape(SSD_GROUPS, SSD_HPG)[..., None] * xs
        y = y.reshape(bsz, seqlen, SSD_WIDTH) * jax.nn.silu(z.astype(f32))
        yg = y.reshape(bsz, seqlen, SSD_GROUPS, SSD_WIDTH // SSD_GROUPS)
        yg = yg * lax.rsqrt(jnp.mean(yg * yg, axis=-1, keepdims=True) + GROUP_EPS)
        ssd_out = yg.reshape(bsz, seqlen, SSD_WIDTH) * ssd_norm_w[l].astype(f32)

        mixed = jnp.concatenate([gla_out, ssd_out], axis=-1).astype(x.dtype)
        x = x + mixed @ w_out[l]

        h2 = rmsnorm(x, norm_ffn_w[l])
        x = x + moe_ffn(h2, router_w[l], router_b[l], moe_w_gate[l], moe_b_gate[l],
                        moe_w_up[l], moe_b_up[l], moe_w_down[l], moe_b_down[l])
    return rmsnorm(x, final_norm_w)


_drawn_inputs = setup_inputs


def setup_inputs(seed=0):
    import zlib

    import numpy as np

    out = dict(_drawn_inputs(seed))
    spreads = {}
    factors = {'gla_norm_w': 2.925,
     'moe_b_gate': 7.698,
     'moe_b_up': 8.0,
     'moe_b_down': 7.262,
     'final_norm_w': 2.91}
    for name, (base, spread) in spreads.items():
        noise = np.random.default_rng([zlib.crc32(name.encode()), seed]).standard_normal(out[name].shape)
        drawn = base * np.exp(spread * noise) if base else spread * noise
        out[name] = __import__('jax').numpy.asarray(drawn.astype(out[name].dtype))
    for name, factor in factors.items():
        out[name] = (out[name] * factor).astype(out[name].dtype)
    return out
```

```python
from contextlib import ExitStack

import numpy as np

import concourse.bass as bass
from concourse import mybir

ALU = mybir.AluOpType
ACT = mybir.ActivationFunctionType
F32 = mybir.dt.float32
I32 = mybir.dt.int32
U32 = mybir.dt.uint32
BF16 = mybir.dt.bfloat16
F32R = mybir.dt.float32r

P = 128
D = 1024
KD = D // P
SEQ = 2048
TILES = SEQ // P
HALF = 512
KW = 256
GW = 512
GH, DK, DV = 4, 64, 128
RANK = 16
SW = 512
SH, SHD, SG, NST = 8, 64, 2, 128
HPG = SH // SG
CH = 1024
TAPS = 4
DIN = 3096
O_QK, O_V, O_G, O_A, O_Z, O_XS, O_BC, O_DT = 0, 512, 1024, 1536, 1552, 2064, 2576, 3088
E = 32
TOPK = 4
F = 1024
LIMIT, ALPHA = 7.0, 1.702
EPS, GEPS = 1e-6, 1e-5
GATE_NORM = 16.0
SLOTS = E * SEQ
BIG = 3.0e38
RING = 4
UNITS = 8
ACTS_AT = 3
ESAT = 1.0e18

N_COLUMNS = (4 + TAPS) * KD
SHARED = [(0, KW), (KW, SH), (KW + SH, SH), (KW + 2 * SH, SH), (KW + 3 * SH, E)]
N_SHARED = KW + 3 * SH + E

STEPS = {
    "act_norm": ["sq", "ln", "rstd", "xn"],
    "pe_in": ["tx", "small", "xs", "bc", "qk", "v", "g", "z"],
    "dve_hT": ["hT"],
    "act_ev": ["xs", "bc", "qk", "v", "g", "z"],
    "dve_dt": ["al", "dtb", "dt", "dta", "ramp"],
    "act_dt": ["abs", "exp", "ln"],
    "pe_gla": ["ta", "zz", "cum", "tqk", "scores", "out", "state"],
    "act_gla": ["alT", "abs", "exp", "ln", "eb", "e1", "e2", "e3", "qkT", "sq", "lnv", "rstd"],
    "dve_gla": ["zb", "la", "q", "k", "ks", "sp", "sc", "dec", "state", "mixed"],
    "pe_ssd": ["txbc", "seg", "tact", "cb", "intra", "inter", "state"],
    "act_ssd": ["xT", "nexp", "nln", "sig", "e16", "tok", "elt", "sq", "lnv", "rstd"],
    "dve_ssd": ["carry", "c0", "c1", "c2", "c3", "sat", "act", "cbm", "m", "xdt", "xw", "y0", "y1",
                "yd", "y2", "y", "dec", "state", "mixed"],
    "act_gz": ["nexp", "nln", "sig"],
    "dve_gz": ["sat", "gz"],
    "pe_out": ["tm", "op0", "op1", "th2", "lg", "rank"],
    "dve_out": ["mT", "x2a", "x2b", "h2T"],
    "act_out": ["sq", "ln", "rstd", "h2"],
    "dve_rt": ["lg", "tok", "top", "neg", "idx", "idxf", "hot", "mask", "rs", "gate", "pos", "hp",
               "slotf", "sloti", "cnt", "tokn"],
    "act_rt": ["exp"],
}
MSTEPS = {
    "pe_gu0": ["c0", "c1", "c2", "c3"],
    "pe_gu1": ["c0", "c1", "c2", "c3"],
    "pe_ta": ["a0", "a1"],
    "pe_tx": ["x0", "x1"],
    "pe_dn": ["c0", "c1", "c2", "c3"],
    "act_hi": [f"u{i}" for i in range(8)],
    "dve_lo": [f"u{i}" for i in range(8)],
    "act_xhi": ["x0", "x1"],
    "dve_xlo": ["x0", "x1"],
    "dve_tab": ["tabm", "tabb"],
    "dve_xT": ["x0", "x1"],
    "dve_a0": ["g", "gm", "u", "um", "p", "a"],
    "dve_a1": ["g", "gm", "u", "um", "p", "a"],
    "act_s": ["s0", "s1"],
    "act_aT": ["a0", "a1"],
    "dve_y": ["y0", "y1"],
    "act_y": ["y"],
}


def build(nc, x, columns, shared, w_in, gla_w_alpha_up, w_out, router_w, moe_w_gate, moe_b_gate, moe_w_up, moe_b_up, moe_w_down, moe_b_down, final_norm_w, out):
    with ExitStack() as ctx:
        def sb(name, shape, dt=F32):
            return ctx.enter_context(nc.sbuf_tensor(name, [P] + shape, dt))

        def ps(name, cols=HALF):
            return ctx.enter_context(nc.psum_tensor(name, [P, cols], F32))

        def sem(name):
            return ctx.enter_context(nc.semaphore(name))

        xacc_d = nc.dram_tensor("xacc_d", [SEQ + P, D], F32, kind="Internal").ap()
        h2_d = nc.dram_tensor("h2_d", [SEQ + P, D], F32, kind="Internal").ap()
        tab_d = nc.dram_tensor("tab_d", [SLOTS, 2], I32, kind="Internal").ap()

        wbig = sb("wbig", [KD * DIN])
        win = wbig[:, :].rearrange("p (k n) -> p k n", k=KD)
        wg = wbig[:, 0:8192].rearrange("p (k n) -> p k n", k=KD)
        wu = wbig[:, 8192:16384].rearrange("p (k n) -> p k n", k=KD)
        wd = wbig[:, 16384:24576].rearrange("p (k n) -> p k n", k=KD)
        wo_t = sb("wo_t", [KD * D])
        wo = wo_t[:, :].rearrange("p (k n) -> p k n", k=KD)
        bg_b, bu_b, bd_b = (wo_t[:, i * D:(i + 1) * D] for i in range(3))
        ident = sb("ident", [P])
        mid2 = sb("mid2", [2])
        cols = sb("cols", [N_COLUMNS])
        nw, mw, fw, cb_ = (cols[:, i * KD:(i + 1) * KD] for i in range(4))
        cw = cols[:, 4 * KD:].rearrange("p (s k) -> p s k", s=TAPS)
        epsx = sb("epsx", [1])
        epsg = sb("epsg", [1])

        mT = sb("mT", [KD, P])
        sto = sb("sto", [4])
        lg = sb("lg", [E]); top = sb("top", [8]); idx = sb("idx", [8], U32); idxf = sb("idxf", [8])
        neg = sb("neg", [1]); ex = sb("ex", [TOPK]); exs = sb("exs", [2])
        hot = sb("hot", [TOPK, E]); mask = sb("mask", [E]); pos = sb("pos", [E])
        cbase = sb("cbase", [E])
        tokf = sb("tokf", [1])
        pair = sb("pair", [TOPK, 2])
        nti = hot[:, 0:2, :].bitcast(I32)
        ends = hot[:, 2, :].bitcast(I32)

        MO = 3 * D
        tab = sb("tab", [2], I32)
        tabm = sb("tabm", [2], I32)
        tabb = sb("tabb", [2], I32)
        gate_op = sb("gate_op", [2])
        xg = wo_t[:, MO:MO + D]
        actT = mT
        act_v = wo_t[:, MO + D:MO + 2 * D]
        gbuf = wo_t[:, MO + 2 * D:MO + 2 * D + HALF]
        sbuf_ = wo_t[:, MO + 2 * D + HALF:MO + 3 * D]
        ubuf = wo_t[:, MO + 3 * D:MO + 3 * D + HALF]
        xraw = [wo_t[:, MO + 3 * D + HALF:MO + 4 * D], sbuf_]
        yout = wo_t[:, MO + 4 * D:MO + 5 * D]

        with ExitStack() as phase_a:
            def pa(name, shape, dt=F32):
                return phase_a.enter_context(nc.sbuf_tensor(name, [P] + shape, dt))

            rw = pa("rw", [KD, E])
            w_up = pa("w_up", [KW])
            m_le = pa("m_le", [P])
            m_gt = pa("m_gt", [P])
            m_mid = pa("m_mid", [P])
            ones = pa("ones", [P])
            iota_e = pa("iota_e", [E])
            iot = pa("iot", [E + 1], I32)
            shr = pa("shr", [N_SHARED])
            ba_b, dtb_b, aneg, dd_b, rb_b = (shr[:, o:o + n] for o, n in SHARED)
            xin = pa("xin", [D])
            junk = pa("junk", [D], BF16)
            st = pa("st", [4])
            hT = pa("hT", [KD, P])
            qk = pa("qk", [HALF])
            v = pa("v", [GW])
            gz = pa("gz", [2, HALF])
            xbc = pa("xbc", [CH])
            al = pa("al", [RANK])
            dt0 = pa("dt0", [SH]); dtl = pa("dtl", [SH])
            dt_ = pa("dt_", [SH]); dta = pa("dta", [SH])
            ramp = pa("ramp", [SH, P])
            elt = pa("elt", [SH, P])
            xT = pa("xT", [KD, P + TAPS - 1])
            cv = pa("cv", [KD, P])
            tok = pa("tok", [SW + SG * NST])
            cbm = pa("cbm", [SG, P])
            xdt = pa("xdt", [SW])
            xw = pa("xw", [SW])
            e16 = pa("e16", [2 * SH])
            yb, yd = qk, xdt
            sst = pa("sst", [SW])
            e1 = pa("e1", [KW]); e2 = pa("e2", [KW]); e3 = pa("e3", [KW])
            alT = e1
            zb, zl, la = e3, e2, e3
            eb = pa("eb", [2, 2])
            qT = pa("qT", [GH, P])
            kT = pa("kT", [2, P])
            sc = pa("sc", [GH, P])
            gst = pa("gst", [2, DV])
            gsp = pa("gsp", [2, DV])
            stg = pa("stg", [3 * GH])
            sts = pa("sts", [3 * SG])
            mixed = pa("mixed", [D])
            xres = pa("xres", [D])
            hp = pa("hp", [TOPK, E]); slotf = pa("slotf", [TOPK]); sloti = pa("sloti", [TOPK], I32)
            nt = hp

        whi = sb("whi", [RING, 2, 2, HALF], F32R)
        wlo = sb("wlo", [RING, 2, 2, HALF], F32R)
        xhi = sb("xhi", [KD, P], F32R)
        xlo = sb("xlo", [KD, P], F32R)

        fin = wbig[:, 0:TILES * D].rearrange("p (t d) -> p t d", t=TILES)
        squares = wbig[:, TILES * D:TILES * D + TILES * D // 2].bitcast(BF16).rearrange("p (t d) -> p t d", t=TILES)
        fst = wo_t[:, D:D + 3 * TILES]

        pp = [ps("pp0"), ps("pp1")]
        tp = ps("tp", 2 * HALF)
        seg = ps("seg", 2 * HALF)
        pg = ps("pg")
        pm = ps("pm")
        p_zz, p_cb = pm[:, 0:256], pm[:, 0:256]
        p_e16, p_eb = pm[:, 256:272], pm[:, 272:276]
        p_lg, p_pre, p_cnt, p_sm = pm[:, 288:320], pm[:, 320:352], pm[:, 352:384], pm[:, 384:408]

        S = {n: sem(n) for n in list(STEPS) + list(MSTEPS)}
        ALLSTEPS = {**STEPS, **MSTEPS}
        where = {f"{s}.{k}": (s, i) for s, ks in ALLSTEPS.items() for i, k in enumerate(ks)}
        turn = {s: 0 for s in ALLSTEPS}

        def done(inst, step):
            s, i = where[step]
            assert turn[s] % len(ALLSTEPS[s]) == i, (step, turn[s])
            turn[s] += 1
            inst.then_inc(S[s], 1)

        def after(eng, step, n):
            s, i = where[step]
            if isinstance(n, int) and n < 0 and s not in MSTEPS:
                return
            first = len(MSTEPS[s]) if s in MSTEPS else 0
            eng.wait_ge(S[s], n * len(ALLSTEPS[s]) + (i + 1 + first))

        d_const = sem("d_const")
        d_win = {c: sem(f"d_win_{c}") for c in ("sm", "xs", "bc", "qk", "v", "g", "z")}
        d_wout = sem("d_wout")
        d_x, d_xres, d_x2, d_h2 = sem("d_x"), sem("d_xres"), sem("d_x2"), sem("d_h2")
        d_tabinit, d_spare, d_slots = sem("d_tabinit"), sem("d_spare"), sem("d_slots")
        setup_p, setup_v, setup_a = sem("setup_p"), sem("setup_v"), sem("setup_a")
        tiles_known = sem("tiles_known")
        d_gu = [[sem(f"d_gu{h}{c}") for c in range(4)] for h in range(2)]
        d_dn = [sem(f"d_dn{c}") for c in range(4)]
        d_bg, d_bu, d_bd = sem("d_bg"), sem("d_bu"), sem("d_bd")
        d_tab, d_gather, d_scatter = sem("d_tab"), sem("d_gather"), sem("d_scatter")
        moe_pool, gate_ran = sem("moe_pool"), sem("gate_ran")
        d_fin, d_fw, d_out = [sem(f"d_fin{c}") for c in range(4)], sem("d_fw"), sem("d_out")
        f_act, f_dve, f_cnt = sem("f_act"), sem("f_dve"), sem("f_cnt")

        block = ctx.enter_context(nc.Block())
        N_CONST = 4
        POOL_SETUP, DVE_SETUP, ACT_SETUP = 11, 15, 1

        def parameters_ready(eng):
            eng.wait_ge(d_const, 16 * N_CONST)
            eng.wait_ge(setup_p, POOL_SETUP)
            eng.wait_ge(setup_v, DVE_SETUP)

        def unit(i):
            h, c = i // 4, i % 4
            return wbig[:, 0:2 * KD * D].rearrange("p (m k n) -> p m k n", m=2, k=KD)[
                :, :, 2 * c:2 * c + 2, h * HALF:(h + 1) * HALF]

        def expert_loops(eng, tile):
            with eng.Fori(0, E) as e:
                first = eng.value_load(ends[0:1, bass.ds(e, 1)], min_val=0, max_val=E + 4 * TILES)
                last = eng.value_load(nti[0:1, 0, bass.ds(e, 1)], min_val=1, max_val=E + 4 * TILES)
                with eng.Fori(first, last) as g:
                    tile(e, g, first)

        @block.sync
        def _(sp):
            sp.dma_start(xin[:, :], x[0, 0:P, :]).then_inc(d_x, 16)
            small = [
                (cols[:, :], columns),
                (shr[:, :], shared[0].partition_broadcast(P)),
                (w_up[0:RANK, :], gla_w_alpha_up[0]),
                (rw[:, :, :], router_w[0].rearrange("(k p) e -> p k e", p=P)),
            ]
            assert len(small) == N_CONST
            for dst, src in small:
                sp.dma_start(dst, src).then_inc(d_const, 16)
            wv = w_in[0].rearrange("(k p) n -> p k n", p=P)
            sp.dma_start(win[:, :, O_A:O_A + RANK], wv[:, :, O_A:O_A + RANK]).then_inc(d_win["sm"], 16)
            sp.dma_start(win[:, :, O_DT:O_DT + SH], wv[:, :, O_DT:O_DT + SH]).then_inc(d_win["sm"], 16)
            for c, o in (("xs", O_XS), ("bc", O_BC), ("qk", O_QK), ("v", O_V), ("g", O_G), ("z", O_Z)):
                sp.dma_start(win[:, :, o:o + HALF], wv[:, :, o:o + HALF]).then_inc(d_win[c], 16)
            sp.dma_start(wo[:, :, :], w_out[0].rearrange("(k p) n -> p k n", p=P)).then_inc(d_wout, 16)

            def gate_up(e, n, h):
                gv = moe_w_gate[0, bass.ds(e, 1)].rearrange("e (k p) f -> p (e k) f", p=P)
                uv = moe_w_up[0, bass.ds(e, 1)].rearrange("e (k p) f -> p (e k) f", p=P)
                fs = slice(h * HALF, (h + 1) * HALF)
                for c in range(4):
                    k2 = slice(2 * c, 2 * c + 2)
                    if not isinstance(n, int):
                        after(sp, f"dve_lo.u{4 * h + c}", n - 1)
                    sp.dma_start(wg[:, k2, fs], gv[:, k2, fs]).then_inc(d_gu[h][c], 16)
                    sp.dma_start(wu[:, k2, fs], uv[:, k2, fs]).then_inc(d_gu[h][c], 16)

            def gate_up_biases(e, n):
                after(sp, "dve_a1.g", n - 1)
                sp.dma_start(bg_b, moe_b_gate[0, bass.ds(e, 1), :].to_broadcast([P, F])).then_inc(d_bg, 16)
                after(sp, "dve_a1.u", n - 1)
                sp.dma_start(bu_b, moe_b_up[0, bass.ds(e, 1), :].to_broadcast([P, F])).then_inc(d_bu, 16)

            def down(e, n):
                dv = moe_w_down[0, bass.ds(e, 1)].rearrange("e (k p) f -> p (e k) f", p=P)
                for c in range(4):
                    k2 = slice(2 * c, 2 * c + 2)
                    after(sp, f"pe_dn.c{c}", n - 1)
                    sp.dma_start(wd[:, k2, :], dv[:, k2, :]).then_inc(d_dn[c], 16)
                after(sp, "dve_y.y1", n - 1)
                sp.dma_start(bd_b, moe_b_down[0, bass.ds(e, 1), :].to_broadcast([P, D])).then_inc(d_bd, 16)

            def body(t, cur=True, lag=True, more=True):
                u = t - 1
                if cur and more:
                    after(sp, "pe_in.tx", t)
                    sp.dma_start(xin[:, :], x[0, bass.ds((t + 1) * P, P), :]).then_inc(d_x, 16)
                if lag:
                    if isinstance(u, int) and u == 0:
                        sp.wait_ge(d_spare, 32)
                    else:
                        sp.wait_ge(d_x2, u * 16)
                        after(sp, "act_out.h2", u - 1)
                    sp.dma_start(xres[:, :], x[0, bass.ds(u * P, P), :]).then_inc(d_xres, 16)
                    if not cur:
                        gate_up(0, 0, 0)
                    after(sp, "dve_out.x2b", u)
                    sp.dma_start(xacc_d[bass.ds(u * P, P), :], xres[:, :]).then_inc(d_x2, 16)
                    after(sp, "act_out.h2", u)
                    sp.dma_start(h2_d[bass.ds(u * P, P), :], mixed[:, :]).then_inc(d_h2, 16)

            body(0, lag=False)
            body(1)
            with sp.Fori(2, TILES - 1) as t:
                body(t)
            body(TILES - 1, more=False)
            after(sp, "pe_in.z", TILES - 1)
            body(TILES, cur=False)
            gate_up(0, 0, 1)
            sp.wait_ge(tiles_known, 1)
            after(sp, "pe_out.op1", TILES - 1)
            gate_up_biases(0, 0)
            sp.wait_ge(d_gather, 16)
            down(0, 0)
            with sp.Fori(1, E) as e:
                n = sp.value_load(ends[0:1, bass.ds(e, 1)], min_val=1, max_val=E + 4 * TILES)
                gate_up(e, n, 0)
                gate_up(e, n, 1)
                gate_up_biases(e, n)
                down(e, n)
            n = sp.value_load(nti[0:1, 0, E - 1:E], min_val=1, max_val=E + 4 * TILES)
            after(sp, "pe_dn.c3", n - 1)
            after(sp, "dve_y.y1", n - 1)
            sp.dma_start(wo_t[:, 0:D], final_norm_w.partition_broadcast(P)).then_inc(d_fw, 16)
            sp.wait_ge(d_scatter, n * 16 + 16)
            for c in range(4):
                sp.dma_start(fin[:, 4 * c:4 * c + 4, :],
                             xacc_d[4 * c * P:4 * (c + 1) * P, :].rearrange("(t p) d -> p t d", p=P)).then_inc(d_fin[c], 16)
            for t in range(TILES):
                sp.wait_ge(f_dve, t + 1)
                sp.dma_start(out[0, t * P:(t + 1) * P, :], fin[:, t, :]).then_inc(d_out, 16)
            sp.wait_ge(d_out, 16 * TILES)

        @block.gpsimd
        def _(pool):
            def made(inst):
                inst.then_inc(setup_p, 1)

            made(pool.memset(ones[:, :], 1.0))
            made(pool.memset(ident[:, :], 0.0))
            made(pool.memset(m_le[:, :], 1.0))
            made(pool.memset(m_gt[:, :], 1.0))
            made(pool.memset(mid2[:, :], 1.0))
            pool.memset(gate_op[:, :], 0.0).then_inc(gate_ran, 1)
            made(pool.iota(iot[:, 0:E], pattern=[[1, E]], base=0, channel_multiplier=0))
            made(pool.iota(iot[:, E:E + 1], pattern=[[0, 1]], base=0, channel_multiplier=1))
            pool.wait_ge(setup_p, 7)
            made(pool.affine_select(out=ident[:, :], in_=ident[:, :], compare_op=ALU.not_equal, fill=1.0,
                                    base=0, pattern=[[-1, P]], channel_multiplier=1))
            made(pool.affine_select(out=m_le[:, :], in_=m_le[:, :], compare_op=ALU.is_ge, fill=0.0,
                                    base=0, pattern=[[1, P]], channel_multiplier=-1))
            made(pool.affine_select(out=m_gt[:, :], in_=m_gt[:, :], compare_op=ALU.is_ge, fill=0.0,
                                    base=-1, pattern=[[-1, P]], channel_multiplier=1))
            made(pool.affine_select(out=mid2[:, 0:1], in_=mid2[:, 0:1], compare_op=ALU.is_ge, fill=0.0,
                                    base=P // 2 - 1, pattern=[[0, 1]], channel_multiplier=-1))
            tini = ramp[:, :, :].rearrange("p a b -> p (a b)").bitcast(I32).rearrange("p (s two) -> p s two", two=2)
            pool.memset(tini, 0).then_inc(moe_pool, 1)
            pool.wait_ge(moe_pool, 1)
            pool.iota(tini[:, :, 0], pattern=[[0, 4], [1, P]], base=SEQ, channel_multiplier=0).then_inc(moe_pool, 1)
            pool.memset(xres[:, :], 0.0).then_inc(moe_pool, 1)
            pool.wait_ge(moe_pool, 3)
            pool.dma_start(tab_d.rearrange("(p s) two -> p (s two)", p=P),
                           tini.rearrange("p s two -> p (s two)")).then_inc(d_tabinit, 16)
            pool.dma_start(xacc_d[SEQ:SEQ + P, :], xres[:, :]).then_inc(d_spare, 16)
            pool.dma_start(h2_d[SEQ:SEQ + P, :], xres[:, :]).then_inc(d_spare, 16)
            pool.wait_ge(d_tabinit, 16)

            def own_wait(n):
                pool.wait_ge(gate_ran, n + 1)
                pool.tensor_tensor(gate_op[0:1, 0:1], gate_op[0:1, 1:2], gate_op[0:1, 1:2],
                                   ALU.add).then_inc(gate_ran, 1)

            def slots(u):
                after(pool, "dve_rt.gate", u)
                after(pool, "dve_rt.sloti", u)
                own_wait(u)
                for k in range(TOPK):
                    pool.indirect_dma_start(
                        out=tab_d, out_offset=bass.IndirectOffsetOnAxis(ap=sloti[:, k:k + 1].bitcast(U32), axis=0),
                        in_=pair[:, k, :].bitcast(I32), in_offset=None).then_inc(d_slots, 16)

            with pool.Fori(0, TILES) as u:
                slots(u)

            pool.wait_ge(d_slots, 16 * TOPK * TILES)
            pool.wait_ge(d_h2, 16 * TILES)
            pool.wait_ge(d_x2, 16 * TILES)
            pool.wait_ge(d_spare, 32)
            pool.wait_ge(tiles_known, 1)

            def fetch(g, row):
                after(pool, "dve_tab.tabm", g - 1)
                own_wait(3 * g + TILES)
                pool.dma_start(tab[:, :], tab_d[bass.ds(row, P), :]).then_inc(d_tab, 16)
                pool.wait_ge(d_tab, g * 16 + 16)
                after(pool, "pe_tx.x1", g - 1)
                own_wait(3 * g + (TILES + 1))
                pool.indirect_dma_start(
                    out=xg, out_offset=None, in_=h2_d,
                    in_offset=bass.IndirectOffsetOnAxis(ap=tab[:, 0:1].bitcast(U32), axis=0)).then_inc(d_gather, 16)

            def add_rows(g):
                after(pool, "act_y.y", g - 1)
                after(pool, "dve_tab.tabb", g - 1)
                own_wait(3 * g + (TILES + 2))
                pool.indirect_dma_start(
                    out=xacc_d, out_offset=bass.IndirectOffsetOnAxis(ap=tabb[:, 0:1].bitcast(U32), axis=0),
                    in_=yout, in_offset=None, compute_op=ALU.add).then_inc(d_scatter, 16)

            def tile(e, g, first):
                fetch(g, nc.s_assert_within(
                    e * SEQ + (g - first) * P, 0, SLOTS - P,
                    skip_runtime_bounds_check_because="an expert has at most SEQ tokens, so at most TILES tiles"))
                add_rows(g)

            expert_loops(pool, tile)
            n = pool.value_load(nti[0:1, 0, E - 1:E], min_val=1, max_val=E + 4 * TILES)
            fetch(n, 0)
            add_rows(n)

        @block.scalar
        def _(act):
            parameters_ready(act)

            def rstd(eng_steps, n, dst, ln, src, scale, eps):
                a, b = eng_steps
                done(act.activation(ln, src, ACT.Ln, bias=eps, scale=scale), a)
                after(act, a, n)
                done(act.activation(dst, ln, ACT.Exp, scale=-0.5), b)
                after(act, b, n)

            def norm(t):
                act.wait_ge(d_x, t * 16 + 16)
                done(act.activation(junk[:, :], xin[:, :], ACT.Square, accum_out=st[:, 0:1]), "act_norm.sq")
                after(act, "act_norm.sq", t)
                rstd(("act_norm.ln", "act_norm.rstd"), t, st[:, 2:3], st[:, 1:2], st[:, 0:1], 1.0 / D, epsx[:, 0:1])
                done(act.activation(xin[:, :], xin[:, :], ACT.Copy, scale=st[:, 2:3]), "act_norm.xn")

            def copy(dst, src, step):
                done(act.activation(dst, src, ACT.Copy), step)

            def body(t, cur=True, lag=True, more=True):
                u = t - 1
                if cur:
                    after(act, "dve_dt.dtb", t)
                    done(act.activation(dtl[:, :], dt0[:, :], ACT.Abs), "act_dt.abs")
                    after(act, "act_dt.abs", t)
                    done(act.activation(dtl[:, :], dtl[:, :], ACT.Exp, scale=-1.0), "act_dt.exp")
                    after(act, "act_dt.exp", t)
                    done(act.activation(dtl[:, :], dtl[:, :], ACT.Ln, bias=1.0), "act_dt.ln")
                    after(act, "pe_in.xs", t)
                    after(act, "dve_ssd.act", t - 1)
                    copy(xbc[:, 0:HALF], pp[0][:, :], "act_ev.xs")
                    after(act, "pe_in.bc", t)
                    copy(xbc[:, HALF:CH], pp[1][:, :], "act_ev.bc")
                    after(act, "pe_ssd.txbc", t)
                    after(act, "dve_ssd.carry", t)
                    copy(xT[:, :, TAPS - 1:], tp[:, :].rearrange("p (k i) -> p k i", k=KD), "act_ssd.xT")
                    after(act, "pe_gla.ta", t)
                    copy(alT[0:RANK, 0:P], tp[0:RANK, 0:P], "act_gla.alT")
                if lag:
                    after(act, "dve_out.x2b", u)
                    done(act.activation(junk[:, :], xres[:, :], ACT.Square, accum_out=sto[:, 0:1]), "act_out.sq")
                    after(act, "act_out.sq", u)
                    rstd(("act_out.ln", "act_out.rstd"), u, sto[:, 2:3], sto[:, 1:2], sto[:, 0:1], 1.0 / D, epsx[:, 0:1])
                    done(act.activation(mixed[:, :], xres[:, :], ACT.Copy, scale=sto[:, 2:3]), "act_out.h2")
                if cur:
                    after(act, "pe_in.qk", t)
                    after(act, "dve_ssd.mixed", t - 1)
                    copy(qk[:, :], pp[0][:, :], "act_ev.qk")
                    after(act, "dve_gla.zb", t)
                    after(act, "pe_gla.tqk", t - 1)
                    done(act.activation(zl[:, :], zb[:, :], ACT.Abs), "act_gla.abs")
                    after(act, "act_gla.abs", t)
                    done(act.activation(zl[:, :], zl[:, :], ACT.Exp, scale=-1.0), "act_gla.exp")
                    after(act, "act_gla.exp", t)
                    done(act.activation(zl[:, :], zl[:, :], ACT.Ln, bias=1.0), "act_gla.ln")
                    after(act, "dve_ssd.c3", t)
                    sg, cvf = xbc[:, :], cv[:, :, :].rearrange("p k i -> p (k i)")
                    done(act.activation(sg, cvf, ACT.Exp, scale=-1.0), "act_ssd.nexp")
                    after(act, "dve_ssd.sat", t)
                    done(act.activation(sg, sg, ACT.Ln, bias=1.0), "act_ssd.nln")
                    after(act, "act_ssd.nln", t)
                    done(act.activation(sg, sg, ACT.Exp, scale=-1.0), "act_ssd.sig")
                    after(act, "pe_in.v", t)
                    after(act, "pe_gla.state", t - 1)
                    copy(v[:, :], pp[1][:, :], "act_ev.v")
                    after(act, "pe_ssd.seg", t)
                    after(act, "dve_ssd.dec", t - 1)
                    done(act.activation(e16[:, :], p_e16, ACT.Exp), "act_ssd.e16")
                    after(act, "pe_gla.cum", t)
                    done(act.activation(eb[:, :, :], p_eb.rearrange("p (a b) -> p a b", a=2), ACT.Exp,
                                        scale=1.0 / GATE_NORM), "act_gla.eb")
                    done(act.activation(e1[:, :], pg[:, 0:KW], ACT.Exp, scale=1.0 / GATE_NORM), "act_gla.e1")
                    done(act.activation(e2[:, :], pg[:, 0:KW], ACT.Exp, scale=-1.0 / GATE_NORM), "act_gla.e2")
                    done(act.activation(e3[:, :], pg[:, KW:], ACT.Exp, scale=1.0 / GATE_NORM), "act_gla.e3")
                if cur:
                    after(act, "pe_gla.tqk", t)
                    q4 = qT[:, :, :].rearrange("p (b h) i -> p b h i", h=2)
                    for h in range(2):
                        r = slice(h * DK, (h + 1) * DK)
                        act.activation(q4[r, :, h, :], tp[r, 0:2 * P].rearrange("p (b i) -> p b i", b=2), ACT.Copy)
                    copy(kT[:, :, :], tp[:, 2 * P:4 * P].rearrange("p (b i) -> p b i", b=2), "act_gla.qkT")
                if lag:
                    after(act, "dve_rt.neg", u)
                    done(act.activation(ex[:, :], top[:, 0:TOPK], ACT.Exp, bias=neg[:, 0:1],
                                        accum_out=exs[:, 0:1]), "act_rt.exp")
                if cur:
                    after(act, "pe_ssd.tact", t)
                    copy(tok[:, :], tp[:, 0:SW + SG * NST], "act_ssd.tok")
                    after(act, "dve_ssd.xw", t - 1)
                    done(act.activation(elt[:, :, :].rearrange("p h i -> p (h i)"), seg[:, :], ACT.Exp), "act_ssd.elt")
                    after(act, "pe_in.g", t)
                    after(act, "dve_gla.mixed", t - 1)
                    copy(gz[:, 0, :], pp[0][:, :], "act_ev.g")
                    after(act, "pe_in.z", t)
                    after(act, "dve_ssd.y", t - 1)
                    copy(gz[:, 1, :], pp[1][:, :], "act_ev.z")
                    after(act, "act_ev.z", t)
                    after(act, "dve_ssd.act", t)
                    gzf = gz[:, :, :].rearrange("p a b -> p (a b)")
                    done(act.activation(xbc[:, :], gzf, ACT.Exp, scale=-1.0), "act_gz.nexp")
                    after(act, "dve_gz.sat", t)
                    done(act.activation(xbc[:, :], xbc[:, :], ACT.Ln, bias=1.0), "act_gz.nln")
                    after(act, "act_gz.nln", t)
                    done(act.activation(xbc[:, :], xbc[:, :], ACT.Exp, scale=-1.0), "act_gz.sig")
                    if more:
                        norm(t + 1)
                    after(act, "pe_gla.out", t)
                    for h in range(GH):
                        i = act.activation(junk[:, h * DV:(h + 1) * DV], pg[:, h * DV:(h + 1) * DV], ACT.Square, accum_out=stg[:, h:h + 1])
                    done(i, "act_gla.sq")
                    after(act, "act_gla.sq", t)
                    rstd(("act_gla.lnv", "act_gla.rstd"), t, stg[:, 8:12], stg[:, 4:8], stg[:, 0:4], 1.0 / DV, epsg[:, 0:1])
                    after(act, "dve_ssd.y", t)
                    for g in range(SG):
                        i = act.activation(junk[:, g * 256:(g + 1) * 256], yb[:, g * 256:(g + 1) * 256], ACT.Square, accum_out=sts[:, g:g + 1])
                    done(i, "act_ssd.sq")
                    after(act, "act_ssd.sq", t)
                    rstd(("act_ssd.lnv", "act_ssd.rstd"), t, sts[:, 4:6], sts[:, 2:4], sts[:, 0:2], 1.0 / 256, epsg[:, 0:1])

            act.activation(aneg, aneg, ACT.Exp).then_inc(setup_a, 1)
            norm(0)
            body(0, lag=False)
            body(1)
            with act.Fori(2, TILES - 1) as t:
                body(t)
            body(TILES - 1, more=False)
            body(TILES, cur=False)

            for s in ("act_s", "act_aT", "act_hi", "act_xhi"):
                act.drain().then_inc(S[s], len(MSTEPS[s]))
            act.wait_ge(tiles_known, 1)
            act.wait_ge(d_x2, 16 * TILES)
            act.wait_ge(d_h2, 16 * TILES)
            act.wait_ge(d_slots, 16 * TOPK * TILES)

            def weights_hi(e, g, units):
                for i in units:
                    act.wait_ge(d_gu[i // 4][i % 4], e * 32 + 32)
                    after(act, f"pe_gu{1 - i // 4}.c{i % 4}", g - 1 if i < RING else g)
                    done(act.activation(whi[:, i % RING], unit(i), ACT.Copy), f"act_hi.u{i}")

            def rows_hi(g):
                for b in range(2):
                    after(act, f"dve_xT.x{b}", g)
                    after(act, "pe_gu1.c3", g - 1)
                    done(act.activation(xhi[:, 4 * b:4 * b + 4, :], xraw[b].rearrange("p (k i) -> p k i", k=4), ACT.Copy),
                         f"act_xhi.x{b}")

            def weigh(g):
                after(act, "dve_y.y1", g)
                done(act.activation(yout, yout, ACT.Copy, scale=tabb[:, 1:2].bitcast(F32)), "act_y.y")

            rows_hi(0)

            def tile(e, g, first):
                weights_hi(e, g, range(0, 4))
                weigh(g - 1)
                weights_hi(e, g, range(4, 8))
                for h in range(2):
                    after(act, f"dve_a{h}.gm", g)
                    if h == 0:
                        after(act, "dve_xlo.x1", g)
                    done(act.activation(sbuf_, gbuf, ACT.Sigmoid, scale=ALPHA), f"act_s.s{h}")
                    if h == 1:
                        rows_hi(g + 1)
                    after(act, f"pe_ta.a{h}", g)
                    done(act.activation(actT[:, 4 * h:4 * h + 4, :],
                                        tp[:, h * HALF:(h + 1) * HALF].rearrange("p (k i) -> p k i", k=4), ACT.Copy),
                         f"act_aT.a{h}")

            expert_loops(act, tile)
            n = act.value_load(nti[0:1, 0, E - 1:E], min_val=1, max_val=E + 4 * TILES)
            weigh(n - 1)
            for t in range(TILES):
                if t % 4 == 0:
                    act.wait_ge(d_fin[t // 4], 16)
                act.activation(squares[:, t, :], fin[:, t, :], ACT.Square, accum_out=fst[:, t:t + 1]).then_inc(f_act, 1)
                if t % 4 == 3:
                    c = slice(t - 3, t + 1)
                    act.wait_ge(f_act, t + 1 + 2 * (t // 4))
                    act.activation(fst[:, TILES:][:, c], fst[:, c], ACT.Ln, bias=epsx[:, 0:1], scale=1.0 / D).then_inc(f_act, 1)
                    act.wait_ge(f_act, t + 2 + 2 * (t // 4))
                    act.activation(fst[:, 2 * TILES:][:, c], fst[:, TILES:][:, c], ACT.Exp, scale=-0.5).then_inc(f_act, 1)

        @block.vector
        def _(dve):
            def set_(inst):
                inst.then_inc(setup_v, 1)

            set_(dve.memset(epsx[:, :], EPS))
            set_(dve.memset(epsg[:, :], GEPS))
            set_(dve.memset(gst[:, :, :], 0.0))
            set_(dve.memset(sst[:, :], 0.0))
            set_(dve.memset(xT[:, :, :], 0.0))
            set_(dve.memset(exs[:, :], 0.0))
            set_(dve.memset(qT[:, :, :], 0.0))
            dve.wait_ge(setup_p, POOL_SETUP)
            dve.wait_ge(d_const, 16 * N_CONST)
            set_(dve.tensor_copy(iota_e[:, :], iot[:, 0:E]))
            set_(dve.tensor_copy(tokf[:, :], iot[:, E:E + 1]))
            set_(dve.tensor_scalar(m_mid[:, :], m_le[:, :], mid2[:, 0:1], None, ALU.subtract))
            dve.wait_ge(setup_v, 9)
            set_(dve.tensor_scalar(cbase[:, :], iota_e[:, :], float(SEQ), -1.0, ALU.mult, ALU.add))
            set_(dve.tensor_scalar(slotf[:, 0:1], tokf[:, :], float(SEQ), None, ALU.add))
            dve.wait_ge(setup_v, 12)
            set_(dve.tensor_copy(tabb[:, 0:1], slotf[:, 0:1]))
            set_(dve.memset(tabb[:, 1:2], 0))
            set_(dve.memset(pm[:, :], 0.0))
            dve.wait_ge(setup_a, ACT_SETUP)
            dve.tensor_scalar(aneg, aneg, -1.0, None, ALU.mult).then_inc(setup_a, 1)
            dve.wait_ge(setup_a, 2)

            def tt(out_, a, b, op, step):
                done(dve.tensor_tensor(out_, a, b, op), step)

            def heads(ap8, n, w):
                return ap8.unsqueeze(2).to_broadcast([P, n, w])

            def over(ap, n):
                return ap.unsqueeze(1).to_broadcast([P, n, ap.shape[-1]])

            def v3(ap, n):
                return ap.rearrange("p (n w) -> p n w", n=n)

            def body(t, cur=True, lag=True):
                u = t - 1
                if cur:
                    after(dve, "pe_in.tx", t)
                    after(dve, "pe_in.z", t - 1)
                    for b in range(2):
                        i = dve.tensor_tensor(hT[:, 4 * b:4 * b + 4, :], v3(tp[:, b * HALF:(b + 1) * HALF], 4),
                                              heads(nw[:, 4 * b:4 * b + 4], 4, P), ALU.mult)
                    done(i, "dve_hT.hT")
                if lag:
                    after(dve, "act_gla.rstd", u)
                    after(dve, "dve_gz.gz", u)
                    if not (isinstance(u, int) and u == 0):
                        dve.wait_ge(d_h2, u * 16)
                        after(dve, "pe_out.th2", u - 1)
                    for h in range(GH):
                        hs = slice(h * DV, (h + 1) * DV)
                        i = dve.scalar_tensor_tensor(out=mixed[:, hs], in0=pg[:, hs], scalar=stg[:, 8 + h:9 + h],
                                                     in1=gz[:, 0, hs], op0=ALU.mult, op1=ALU.mult)
                    done(i, "dve_gla.mixed")
                    after(dve, "act_ssd.rstd", u)
                    for g in range(SG):
                        gs = slice(g * 256, (g + 1) * 256)
                        i = dve.tensor_scalar(mixed[:, GW + g * 256:GW + (g + 1) * 256], yb[:, gs],
                                              sts[:, 4 + g:5 + g], None, ALU.mult)
                    done(i, "dve_ssd.mixed")
                if cur:
                    after(dve, "pe_in.small", t)
                    done(dve.tensor_copy(al[:, :], p_sm[:, 0:RANK]), "dve_dt.al")
                    tt(dt0[:, :], p_sm[:, RANK:RANK + SH], dtb_b, ALU.add, "dve_dt.dtb")
                    after(dve, "act_ssd.xT", t - 1)
                    after(dve, "dve_ssd.c3", t - 1)
                    done(dve.tensor_copy(xT[:, :, 0:TAPS - 1], xT[:, :, P:]), "dve_ssd.carry")
                    after(dve, "act_dt.ln", t)
                    done(dve.scalar_tensor_tensor(out=dt_[:, :], in0=dt0[:, :], scalar=0.0, in1=dtl[:, :],
                                                  op0=ALU.max, op1=ALU.add), "dve_dt.dt")
                    after(dve, "dve_dt.dt", t)
                    after(dve, "pe_ssd.seg", t - 1)
                    tt(dta[:, :], dt_[:, :], aneg, ALU.mult, "dve_dt.dta")
                    after(dve, "dve_dt.dta", t)
                    if isinstance(t, int) and t == 0:
                        dve.wait_ge(d_tabinit, 16)
                    after(dve, "pe_ssd.intra", t - 1)
                    tt(ramp[:, :, :], over(m_le[:, :], SH), heads(dta[:, :], SH, P), ALU.mult, "dve_dt.ramp")
                if lag:
                    after(dve, "pe_out.tm", u)
                    after(dve, "pe_out.lg", u - 1)
                    for b in range(2):
                        i = dve.tensor_tensor(mT[:, 4 * b:4 * b + 4, :], v3(tp[:, b * HALF:(b + 1) * HALF], 4),
                                              heads(mw[:, 4 * b:4 * b + 4], 4, P), ALU.mult)
                    done(i, "dve_out.mT")
                if cur:
                    after(dve, "act_ssd.xT", t)
                    after(dve, "dve_ssd.carry", t)
                    after(dve, "pe_ssd.tact", t - 1)
                    after(dve, "pe_ssd.inter", t - 1)
                    for s in range(TAPS):
                        for k in range(KD):
                            src = xT[:, k, TAPS - 1 - s:TAPS - 1 - s + P]
                            w = cw[:, TAPS - 1 - s, k:k + 1]
                            if s == 0:
                                i = dve.tensor_scalar(cv[:, k, :], src, w, cb_[:, k:k + 1], ALU.mult, ALU.add)
                            else:
                                i = dve.scalar_tensor_tensor(out=cv[:, k, :], in0=src, scalar=w, in1=cv[:, k, :],
                                                             op0=ALU.mult, op1=ALU.add)
                        done(i, f"dve_ssd.c{s}")
                        after(dve, f"dve_ssd.c{s}", t)
                if lag:
                    dve.wait_ge(d_xres, u * 16 + 16)
                    after(dve, "pe_out.op0", u)
                    tt(xres[:, 0:HALF], pp[0][:, :], xres[:, 0:HALF], ALU.add, "dve_out.x2a")
                    after(dve, "pe_out.op1", u)
                    tt(xres[:, HALF:D], pp[1][:, :], xres[:, HALF:D], ALU.add, "dve_out.x2b")
                if cur:
                    after(dve, "pe_gla.zz", t)
                    after(dve, "pe_gla.state", t - 1)
                    tt(zb[:, :], p_zz, ba_b, ALU.add, "dve_gla.zb")
                    after(dve, "act_ssd.nexp", t)
                    done(dve.tensor_scalar(xbc[:, :], xbc[:, :], ESAT, None, ALU.min), "dve_ssd.sat")
                    after(dve, "act_gla.ln", t)
                    after(dve, "pe_gla.cum", t - 1)
                    done(dve.scalar_tensor_tensor(out=la[:, :], in0=zb[:, :], scalar=0.0, in1=zl[:, :],
                                                  op0=ALU.min, op1=ALU.subtract), "dve_gla.la")
                    after(dve, "act_ssd.sig", t)
                    cvf = cv[:, :, :].rearrange("p k i -> p (k i)")
                    tt(cvf, cvf, xbc[:, :], ALU.mult, "dve_ssd.act")
                if lag:
                    after(dve, "pe_out.th2", u)
                    for b in range(2):
                        i = dve.tensor_tensor(mT[:, 4 * b:4 * b + 4, :], v3(tp[:, b * HALF:(b + 1) * HALF], 4),
                                              heads(fw[:, 4 * b:4 * b + 4], 4, P), ALU.mult)
                    done(i, "dve_out.h2T")
                if cur:
                    after(dve, "act_gla.e3", t)
                    after(dve, "act_ev.qk", t)
                    done(dve.scalar_tensor_tensor(out=e1[:, :], in0=qk[:, 0:KW], scalar=DK ** -0.5, in1=e1[:, :],
                                                  op0=ALU.mult, op1=ALU.mult), "dve_gla.q")
                    tt(e2[:, :], qk[:, KW:], e2[:, :], ALU.mult, "dve_gla.k")
                    tt(e3[:, :], qk[:, KW:], e3[:, :], ALU.mult, "dve_gla.ks")
                    after(dve, "dve_gla.state", t - 1)
                    tt(gsp[:, :, :], gst[:, :, :], eb[:, :, 0:1].to_broadcast([P, 2, DV]), ALU.mult, "dve_gla.sp")
                if lag:
                    R = "dve_rt."
                    after(dve, "pe_out.lg", u)
                    tt(lg[:, :], p_lg, rb_b, ALU.add, R + "lg")
                    if not (isinstance(u, int) and u == 0):
                        dve.wait_ge(d_slots, u * (16 * TOPK))
                    after(dve, R + "lg", u)
                    done(dve.tensor_copy(pair[:, :, 0].bitcast(I32), tokf[:, :].to_broadcast([P, TOPK])), R + "tok")
                    done(dve.max(out=top[:, :], in_=lg[:, :]), R + "top")
                    after(dve, R + "top", u)
                    done(dve.tensor_scalar(neg[:, :], top[:, 0:1], -1.0, None, ALU.mult), R + "neg")
                    done(dve.max_index(out=idx[:, :], in_max=top[:, :], in_values=lg[:, :]), R + "idx")
                    after(dve, R + "idx", u)
                    done(dve.tensor_copy(idxf[:, :], idx[:, :]), R + "idxf")
                    after(dve, R + "idxf", u)
                    tt(hot[:, :, :], over(iota_e[:, :], TOPK), heads(idxf[:, 0:TOPK], TOPK, E), ALU.is_equal, R + "hot")
                    after(dve, R + "hot", u)
                    done(dve.tensor_reduce(mask[:, :], hot[:, :, :].rearrange("p k e -> p e k"),
                                           mybir.AxisListType.X, ALU.add), R + "mask")
                    after(dve, "act_rt.exp", u)
                    done(dve.reciprocal(exs[:, 1:2], exs[:, 0:1]), R + "rs")
                    after(dve, R + "rs", u)
                    done(dve.tensor_scalar(pair[:, :, 1], ex[:, :], exs[:, 1:2], None, ALU.mult), R + "gate")
                    after(dve, "pe_out.rank", u)
                    tt(pos[:, :], p_pre, cbase[:, :], ALU.add, R + "pos")
                    after(dve, R + "pos", u)
                    tt(hp[:, :, :], hot[:, :, :], over(pos[:, :], TOPK), ALU.mult, R + "hp")
                    after(dve, R + "hp", u)
                    done(dve.tensor_reduce(slotf[:, :], hp[:, :, :], mybir.AxisListType.X, ALU.add), R + "slotf")
                    after(dve, R + "slotf", u)
                    done(dve.tensor_copy(sloti[:, :], slotf[:, :]), R + "sloti")
                    tt(cbase[:, :], p_cnt, cbase[:, :], ALU.add, R + "cnt")
                    after(dve, R + "tok", u)
                    done(dve.tensor_scalar(tokf[:, :], tokf[:, :], float(P), None, ALU.add), R + "tokn")
                if cur:
                    after(dve, "pe_gla.scores", t)
                    done(dve.scalar_tensor_tensor(out=sc[:, :, :], in0=v3(pg[:, :], GH), scalar=BIG,
                                                  in1=over(m_le[:, :], GH), op0=ALU.min, op1=ALU.mult), "dve_gla.sc")
                    after(dve, "act_gz.nexp", t)
                    done(dve.tensor_scalar(xbc[:, :], xbc[:, :], ESAT, None, ALU.min), "dve_gz.sat")
                    after(dve, "pe_ssd.cb", t)
                    tt(cbm[:, :, :], v3(p_cb, SG), over(m_le[:, :], SG), ALU.mult, "dve_ssd.cbm")
                    after(dve, "act_ssd.elt", t)
                    after(dve, "dve_ssd.cbm", t)
                    r4 = ramp[:, :, :].rearrange("p (g h) i -> p g h i", g=SG)
                    tt(r4, elt[:, :, :].rearrange("p (g h) i -> p g h i", g=SG),
                       cbm[:, :, :].unsqueeze(2).to_broadcast([P, SG, HPG, P]), ALU.mult, "dve_ssd.m")
                    after(dve, "act_ssd.tok", t)
                    tt(v3(xdt[:, :], SH), v3(tok[:, 0:SW], SH), heads(dt_[:, :], SH, SHD), ALU.mult, "dve_ssd.xdt")
                    after(dve, "dve_ssd.xdt", t)
                    tt(v3(xw[:, :], SH), v3(xdt[:, :], SH), elt[:, :, P - 1:P].to_broadcast([P, SH, SHD]), ALU.mult,
                       "dve_ssd.xw")
                    after(dve, "act_gz.sig", t)
                    tt(gz[:, :, :].rearrange("p a b -> p (a b)"), gz[:, :, :].rearrange("p a b -> p (a b)"), xbc[:, :],
                       ALU.mult, "dve_gz.gz")
                    after(dve, "pe_ssd.inter", t)
                    tt(v3(yb[:, :], SH), v3(seg[:, HALF:], SH), heads(e16[:, 0:SH], SH, SHD), ALU.mult, "dve_ssd.y0")
                    after(dve, "dve_ssd.y0", t)
                    tt(yb[:, :], seg[:, 0:HALF], yb[:, :], ALU.add, "dve_ssd.y1")
                    tt(v3(yd[:, :], SH), v3(tok[:, 0:SW], SH), heads(dd_b, SH, SHD), ALU.mult, "dve_ssd.yd")
                    after(dve, "dve_ssd.yd", t)
                    tt(yb[:, :], yb[:, :], yd[:, :], ALU.add, "dve_ssd.y2")
                    after(dve, "dve_ssd.y2", t)
                    after(dve, "dve_gz.gz", t)
                    tt(yb[:, :], yb[:, :], gz[:, 1, :], ALU.mult, "dve_ssd.y")
                    tt(gst[:, :, :], gst[:, :, :], eb[:, :, 1:2].to_broadcast([P, 2, DV]), ALU.mult, "dve_gla.dec")
                    after(dve, "dve_gla.dec", t)
                    after(dve, "pe_gla.state", t)
                    for b in range(2):
                        for h in range(2):
                            r = slice(h * DK, (h + 1) * DK)
                            c = b * 256 + h * DV
                            i = dve.tensor_tensor(gst[r, b, :], pp[0][r, c:c + DV], gst[r, b, :], ALU.add)
                    done(i, "dve_gla.state")
                    tt(v3(sst[:, :], SH), v3(sst[:, :], SH), heads(e16[:, SH:2 * SH], SH, SHD), ALU.mult, "dve_ssd.dec")
                    after(dve, "dve_ssd.dec", t)
                    after(dve, "pe_ssd.state", t)
                    tt(sst[:, :], seg[:, HALF:], sst[:, :], ALU.add, "dve_ssd.state")

            body(0, lag=False)
            body(1)
            with dve.Fori(2, TILES) as t:
                body(t)
            body(TILES, cur=False)

            cnt_steps = [0]

            def step(inst):
                inst.then_inc(f_cnt, 1)
                cnt_steps[0] += 1
                dve.wait_ge(f_cnt, cnt_steps[0])

            after(dve, "dve_rt.cnt", TILES - 1)
            step(dve.scalar_tensor_tensor(out=nt[:, 0, :], in0=iota_e[:, :], scalar=-float(SEQ), in1=cbase[:, :],
                                          op0=ALU.mult, op1=ALU.add))
            step(dve.tensor_scalar(nt[:, 0, :], nt[:, 0, :], float(P), None, ALU.add))
            step(dve.tensor_copy(nti[:, 1, :], nt[:, 0, :]))
            step(dve.tensor_scalar(nti[:, 0, :], nti[:, 1, :], 7, None, ALU.arith_shift_right))
            step(dve.tensor_copy(nt[:, 1, :], nti[:, 0, :]))
            step(dve.tensor_scalar(nt[:, 0, :], nt[:, 1, :], 1.0, None, ALU.max))
            step(dve.tensor_tensor_scan(nt[:, 1, :], ones[:, 0:E], nt[:, 0, :], 0.0, ALU.mult, ALU.add))
            step(dve.tensor_tensor(nt[:, 2, :], nt[:, 1, :], nt[:, 0, :], ALU.subtract))
            step(dve.tensor_copy(ends, nt[:, 2, :]))
            step(dve.tensor_copy(nti[:, 0, :], nt[:, 1, :]))
            for eng_wait in range(1):
                dve.drain().then_inc(tiles_known, 1)
            after(dve, "pe_out.op1", TILES - 1)
            for s in ("dve_tab", "dve_xT", "dve_a0", "dve_a1", "dve_lo", "dve_xlo"):
                dve.drain().then_inc(S[s], len(MSTEPS[s]))

            def rows_T(g):
                for b in range(2):
                    after(dve, f"pe_tx.x{b}", g)
                    after(dve, f"dve_xlo.x{b}", g - 1)
                    if b == 1:
                        after(dve, "dve_a1.a", g - 1)
                    tt(xraw[b].rearrange("p (k i) -> p k i", k=4), v3(tp[:, b * HALF:(b + 1) * HALF], 4),
                       heads(fw[:, 4 * b:4 * b + 4], 4, P), ALU.mult, f"dve_xT.x{b}")

            def rows_lo(g):
                for b in range(2):
                    kb = slice(4 * b, 4 * b + 4)
                    after(dve, f"act_xhi.x{b}", g)
                    tt(xlo[:, kb, :], xraw[b].rearrange("p (k i) -> p k i", k=4), xhi[:, kb, :].bitcast(F32),
                       ALU.subtract, f"dve_xlo.x{b}")

            def weights_lo(g, units):
                for i in units:
                    after(dve, f"act_hi.u{i}", g)
                    tt(wlo[:, i % RING], unit(i), whi[:, i % RING].bitcast(F32), ALU.subtract, f"dve_lo.u{i}")

            def add_bias(g):
                after(dve, "pe_dn.c3", g)
                tt(yout[:, 0:HALF], pg[:, :], bd_b[:, 0:HALF], ALU.add, "dve_y.y0")
                tt(yout[:, HALF:], pm[:, :], bd_b[:, HALF:], ALU.add, "dve_y.y1")

            rows_T(0)
            rows_lo(0)

            def tile(e, g, first):
                dve.wait_ge(d_tab, g * 16 + 16)
                after(dve, "dve_tab.tabb", g - 1)
                done(dve.tensor_copy(tabm[:, :], tab[:, :]), "dve_tab.tabm")
                weights_lo(g, range(0, 2))
                add_bias(g - 1)
                weights_lo(g, range(2, 7))
                for h in range(2):
                    hs = slice(h * HALF, (h + 1) * HALF)
                    pgate, pup = (pp[0][:, :], pp[1][:, :]) if h == 0 else (seg[:, 0:HALF], seg[:, HALF:])
                    A = f"dve_a{h}."
                    after(dve, f"pe_gu{h}.c3", g)
                    dve.wait_ge(d_bg, e * 16 + 16)
                    tt(gbuf, pgate, bg_b[:, hs], ALU.add, A + "g")
                    after(dve, A + "g", g)
                    done(dve.tensor_scalar(gbuf, gbuf, LIMIT, None, ALU.min), A + "gm")
                    if h == 0:
                        weights_lo(g, range(7, 8))
                    dve.wait_ge(d_bu, e * 16 + 16)
                    tt(ubuf, pup, bu_b[:, hs], ALU.add, A + "u")
                    after(dve, A + "u", g)
                    done(dve.tensor_scalar(ubuf, ubuf, LIMIT, -LIMIT, ALU.min, ALU.max), A + "um")
                    after(dve, A + "um", g)
                    done(dve.scalar_tensor_tensor(out=ubuf, in0=ubuf, scalar=1.0, in1=gbuf,
                                                  op0=ALU.add, op1=ALU.mult), A + "p")
                    after(dve, A + "p", g)
                    after(dve, f"act_s.s{h}", g)
                    after(dve, f"pe_ta.a{h}", g - 1)
                    tt(act_v[:, hs], ubuf, sbuf_, ALU.mult, A + "a")
                    if h == 0:
                        after(dve, "dve_tab.tabm", g)
                        dve.wait_ge(d_scatter, g * 16 + 16)
                        done(dve.tensor_copy(tabb[:, :], tabm[:, :]), "dve_tab.tabb")
                        dve.wait_ge(d_bd, e * 16 + 16)
                rows_T(g + 1)
                rows_lo(g + 1)

            expert_loops(dve, tile)
            n = dve.value_load(nti[0:1, 0, E - 1:E], min_val=1, max_val=E + 4 * TILES)
            add_bias(n - 1)
            dve.wait_ge(d_fw, 16)
            for t in range(TILES):
                dve.wait_ge(f_act, 6 * (t // 4 + 1))
                dve.scalar_tensor_tensor(out=fin[:, t, :], in0=fin[:, t, :], scalar=fst[:, 2 * TILES + t:2 * TILES + t + 1],
                                         in1=wo_t[:, 0:D], op0=ALU.mult, op1=ALU.mult).then_inc(f_dve, 1)

        @block.tensor
        def _(pe):
            parameters_ready(pe)

            def transposes(blocks, src, step, rows=P):
                for b in range(blocks):
                    i = pe.transpose(tp[:, b * P:(b + 1) * P], src(b), ident[:, :])
                done(i, step)

            def project(dst, w, o, n, lhs):
                for k in range(KD):
                    i = pe.matmul(dst, lhs[:, k, :], w[:, k, o:o + n], start=(k == 0), stop=(k == KD - 1))
                return i

            def chunk(t, name, bank, o):
                if isinstance(t, int) and t == 0:
                    pe.wait_ge(d_win[name], 16)
                done(project(pp[bank][:, :], win, o, HALF, hT), f"pe_in.{name}")

            def body(t, cur=True, lag=True):
                u = t - 1
                if cur:
                    after(pe, "act_norm.xn", t)
                    after(pe, "act_ssd.tok", t - 1)
                    transposes(8, lambda b: xin[:, b * P:(b + 1) * P], "pe_in.tx")
                    after(pe, "dve_hT.hT", t)
                    if isinstance(t, int) and t == 0:
                        pe.wait_ge(d_win["sm"], 32)
                    after(pe, "dve_ssd.cbm", t - 1)
                    project(p_sm[:, 0:RANK], win, O_A, RANK, hT)
                    done(project(p_sm[:, RANK:RANK + SH], win, O_DT, SH, hT), "pe_in.small")
                    after(pe, "dve_gla.state", t - 1)
                    chunk(t, "xs", 0, O_XS)
                if lag:
                    after(pe, "dve_gla.mixed", u)
                    after(pe, "dve_ssd.mixed", u)
                    after(pe, "dve_hT.hT" if cur else "act_ssd.tok", t if cur else u)
                    transposes(8, lambda b: mixed[:, b * P:(b + 1) * P], "pe_out.tm")
                if cur:
                    after(pe, "act_ev.z", t - 1)
                    chunk(t, "bc", 1, O_BC)
                    after(pe, "act_ev.xs", t)
                    after(pe, "act_ev.bc", t)
                    after(pe, "dve_out.mT" if lag else "dve_hT.hT", u if lag else t)
                    transposes(8, lambda b: xbc[:, b * P:(b + 1) * P], "pe_ssd.txbc")
                if lag:
                    after(pe, "dve_out.mT", u)
                    if isinstance(u, int) and u == 0:
                        pe.wait_ge(d_wout, 16)
                    after(pe, "act_ev.xs" if cur else "dve_gla.state", t if cur else u)
                    done(project(pp[0][:, :], wo, 0, HALF, mT), "pe_out.op0")
                if cur:
                    after(pe, "act_ssd.xT", t)
                    after(pe, "dve_dt.al", t)
                    i = pe.transpose(tp[0:RANK, 0:P], al[:, :], ident[:, :])
                    done(i, "pe_gla.ta")
                if lag:
                    after(pe, "act_ev.bc" if cur else "act_ev.z", t if cur else u)
                    done(project(pp[1][:, :], wo, HALF, HALF, mT), "pe_out.op1")
                if cur:
                    after(pe, "dve_out.x2a" if lag else "act_ev.xs", u if lag else t)
                    chunk(t, "qk", 0, O_QK)
                    after(pe, "act_gla.alT", t)
                    after(pe, "dve_dt.dtb", t)
                    i = pe.matmul(p_zz, alT[0:RANK, 0:P], w_up[0:RANK, :], start=True, stop=True)
                    done(i, "pe_gla.zz")
                    after(pe, "dve_out.x2b" if lag else "act_ev.bc", u if lag else t)
                    chunk(t, "v", 1, O_V)
                    after(pe, "dve_dt.ramp", t)
                    after(pe, "dve_gla.zb", t)
                    after(pe, "dve_ssd.state", t - 1)
                    for b in range(2):
                        i = pe.matmul(seg[:, b * HALF:(b + 1) * HALF], m_gt[:, :],
                                      ramp[:, 4 * b:4 * b + 4, :].rearrange("p h i -> p (h i)"), start=True, stop=True)
                    pe.matmul(p_e16[:, 0:SH], m_le[:, :], dta[:, :], start=True, stop=True)
                    i = pe.matmul(p_e16[:, SH:2 * SH], ones[:, :], dta[:, :], start=True, stop=True)
                    done(i, "pe_ssd.seg")
                if lag:
                    after(pe, "act_out.h2", u)
                    transposes(8, lambda b: mixed[:, b * P:(b + 1) * P], "pe_out.th2")
                if cur:
                    after(pe, "act_ev.qk", t)
                    chunk(t, "g", 0, O_G)
                    after(pe, "dve_gla.la", t)
                    after(pe, "dve_gla.mixed", t - 1)
                    pe.matmul(pg[:, 0:KW], m_mid[:, :], la[:, :], start=True, stop=True)
                    pe.matmul(pg[:, KW:], m_gt[:, :], la[:, :], start=True, stop=True)
                    after(pe, "act_ssd.e16", t)
                    for b in range(2):
                        i = pe.matmul(p_eb[:, 2 * b:2 * b + 2], la[:, b * P:(b + 1) * P], mid2[:, :], start=True, stop=True)
                    done(i, "pe_gla.cum")
                if lag:
                    after(pe, "dve_out.h2T", u)
                    after(pe, "act_gla.eb" if cur else "dve_ssd.cbm", t if cur else u)
                    for k in range(KD):
                        i = pe.matmul(p_lg, mT[:, k, :], rw[:, k, :], start=(k == 0), stop=(k == KD - 1))
                    done(i, "pe_out.lg")
                if cur:
                    after(pe, "dve_gla.q", t)
                    after(pe, "dve_gla.k", t)
                    after(pe, "dve_out.h2T" if lag else "act_gla.alT", u if lag else t)
                    transposes(4, lambda b: (e1, e1, e2, e2)[b][:, (b % 2) * P:(b % 2 + 1) * P], "pe_gla.tqk")
                    after(pe, "act_gla.qkT", t)
                    after(pe, "dve_ssd.act", t)
                    transposes(6, lambda b: cv[:, b, :], "pe_ssd.tact")
                    after(pe, "act_ev.v", t)
                    chunk(t, "z", 1, O_Z)
                if lag:
                    after(pe, "dve_rt.mask", u)
                    pe.matmul(p_pre, m_le[:, :], mask[:, :], start=True, stop=True)
                    i = pe.matmul(p_cnt, ones[:, :], mask[:, :], start=True, stop=True)
                    done(i, "pe_out.rank")
                if cur:
                    after(pe, "act_gla.e3", t)
                    for h in range(GH):
                        i = pe.matmul(pg[:, h * P:(h + 1) * P], kT[:, h // 2, :], qT[:, h, :],
                                      start=True, stop=True)
                    done(i, "pe_gla.scores")
                    after(pe, "dve_rt.cnt" if lag else "act_gla.eb", u if lag else t)
                    for g in range(SG):
                        i = pe.matmul(p_cb[:, g * P:(g + 1) * P], cv[:, 4 + g, :], cv[:, 6 + g, :], start=True, stop=True)
                    done(i, "pe_ssd.cb")
                    after(pe, "dve_gla.sc", t)
                    after(pe, "dve_gla.sp", t)
                    after(pe, "act_ev.v", t)
                    for h in range(GH):
                        hs = slice(h * DV, (h + 1) * DV)
                        pe.matmul(pg[:, hs], sc[:, h, :], v[:, hs], start=True, stop=False)
                        i = pe.matmul(pg[:, hs], qT[:, h, :], gsp[:, h // 2, :], start=False, stop=True)
                    done(i, "pe_gla.out")
                    after(pe, "dve_ssd.m", t)
                    after(pe, "dve_ssd.xdt", t)
                    for h in range(SH):
                        hs = slice(h * SHD, (h + 1) * SHD)
                        i = pe.matmul(seg[:, hs], ramp[:, h, :], xdt[:, hs], start=True, stop=True)
                    done(i, "pe_ssd.intra")
                    after(pe, "dve_ssd.state", t - 1)
                    for g in range(SG):
                        gs = slice(g * 256, (g + 1) * 256)
                        i = pe.matmul(seg[:, HALF + g * 256:HALF + (g + 1) * 256], cv[:, 6 + g, :], sst[:, gs],
                                      start=True, stop=True)
                    done(i, "pe_ssd.inter")
                    after(pe, "dve_ssd.y0", t)
                    after(pe, "dve_ssd.xw", t)
                    for g in range(SG):
                        gs = slice(g * 256, (g + 1) * 256)
                        i = pe.matmul(seg[:, HALF + g * 256:HALF + (g + 1) * 256],
                                      tok[:, SW + g * NST:SW + (g + 1) * NST], xw[:, gs], start=True, stop=True)
                    done(i, "pe_ssd.state")
                    after(pe, "dve_gla.ks", t)
                    after(pe, "act_ev.g", t)
                    for b in range(2):
                        i = pe.matmul(pp[0][:, b * 256:(b + 1) * 256], e3[:, b * P:(b + 1) * P],
                                      v[:, b * 256:(b + 1) * 256], start=True, stop=True)
                    done(i, "pe_gla.state")

            body(0, lag=False)
            body(1)
            with pe.Fori(2, TILES) as t:
                body(t)
            body(TILES, cur=False)
            for s in ("pe_gu0", "pe_gu1", "pe_ta", "pe_tx", "pe_dn"):
                pe.drain().then_inc(S[s], len(MSTEPS[s]))

            def rows(g, b):
                if b == 0:
                    pe.wait_ge(d_gather, g * 16 + 16)
                for k in range(4):
                    kk = 4 * b + k
                    i = pe.transpose(tp[:, kk * P:(kk + 1) * P], xg[:, kk * P:(kk + 1) * P], ident[:, :])
                done(i, f"pe_tx.x{b}")

            rows(0, 0)
            rows(0, 1)

            def acts(h):
                for k in range(4 * h, 4 * h + 4):
                    i = pe.transpose(tp[:, k * P:(k + 1) * P], act_v[:, k * P:(k + 1) * P], ident[:, :])
                done(i, f"pe_ta.a{h}")

            pe.wait_ge(tiles_known, 1)

            def tile(e, g, first):
                after(pe, "dve_xlo.x1", g)
                for i in range(UNITS):
                    h, c, r = i // 4, i % 4, i % RING
                    bank = (pp[0][:, :], pp[1][:, :]) if h == 0 else (seg[:, 0:HALF], seg[:, HALF:])
                    if c == 0:
                        after(pe, f"dve_a{h}.u", g - 1)
                    after(pe, f"dve_lo.u{i}", g)
                    for k in range(2):
                        kk = 2 * c + k
                        for x_part, w_part, first_part, last_part in ((xhi, whi, True, False), (xhi, wlo, False, False),
                                                                      (xlo, whi, False, True)):
                            for m in range(2):
                                j = pe.matmul(bank[m], x_part[:, kk, :], w_part[:, r, m, k, :],
                                              start=(kk == 0 and first_part), stop=(kk == KD - 1 and last_part))
                    done(j, f"pe_gu{h}.c{c}")
                    if i == 6:
                        after(pe, "dve_a0.a", g)
                        acts(0)
                after(pe, "act_aT.a0", g)
                rows(g + 1, 0)
                after(pe, "act_aT.a1", g - 1)
                rows(g + 1, 1)
                after(pe, "dve_y.y1", g - 1)
                for k in range(KD):
                    if k == ACTS_AT:
                        after(pe, "dve_a1.a", g)
                        after(pe, "dve_xT.x1", g + 1)
                        acts(1)
                    if k == 4:
                        after(pe, "act_aT.a1", g)
                    if k % 2 == 0:
                        pe.wait_ge(d_dn[k // 2], e * 16 + 16)
                    pe.matmul(pg[:, :], actT[:, k, :], wd[:, k, 0:HALF], start=(k == 0), stop=(k == KD - 1))
                    i = pe.matmul(pm[:, :], actT[:, k, :], wd[:, k, HALF:], start=(k == 0), stop=(k == KD - 1))
                    if k % 2:
                        done(i, f"pe_dn.c{k // 2}")

            expert_loops(pe, tile)


_INS = ["x", "columns", "shared", "w_in", "gla_w_alpha_up", "w_out", "router_w", "moe_w_gate", "moe_b_gate",
        "moe_w_up", "moe_b_up", "moe_w_down", "moe_b_down", "final_norm_w"]


def kernel(**inputs):
    import numpy as _np
    import concourse.bacc as _bacc
    from concourse import mybir as _mybir
    from concourse.bass_utils import run_bass_kernel_spmd as _run

    vectors = [inputs["norm_mix_w"][0], inputs["gla_norm_w"][0], inputs["ssd_norm_w"][0], inputs["norm_ffn_w"][0],
               inputs["ssd_conv_b"][0], *inputs["ssd_conv_w"][0]]
    columns = _np.concatenate([_np.asarray(a).reshape(-1, P).T for a in vectors], axis=1)
    shared = _np.concatenate([_np.asarray(inputs[n][0]) for n in
                              ("gla_b_alpha", "ssd_dt_bias", "ssd_A_log", "ssd_D", "router_b")])[None]
    inputs = {**inputs, "columns": columns, "shared": shared}

    nc = _bacc.Bacc("TRN2", target_bir_lowering=False, num_devices=1)
    arrays, args = {}, []
    for name in _INS:
        a = _np.ascontiguousarray(inputs[name])
        arrays[f"in_{name}"] = a
        args.append(nc.dram_tensor(f"in_{name}", a.shape, _mybir.dt.from_np(a.dtype), kind="ExternalInput").ap())
    args.append(nc.dram_tensor("out_0", (1, SEQ, D), _mybir.dt.float32, kind="ExternalOutput").ap())
    build(nc, *args)
    r = _run(nc, [arrays], core_ids=[0])
    return r.results[0]["out_0"]
```
